# Optimizing a Trainium2 kernel written in Bass

```python
import math
import jax, jax.numpy as jnp
from jax import lax
import numpy as np

D_MODEL = 1024
BATCH = 1
SEQ = 512
DEPTH = 2

N_MIXERS = 2
N_A_LAYERS = (DEPTH + 1) // 2
N_B_LAYERS = DEPTH // 2
DA_HEADS = 8
DA_HEAD_DIM = 64
DA_V_DIM = 2 * DA_HEAD_DIM
Q_BLOCK = 128
REL_BUCKETS = 32
REL_MAX_EXACT = REL_BUCKETS // 2
REL_MAX_DIST = 128
SGU_CHUNK = 128
SGU_WIDTH = D_MODEL
SGU_GROUPS = 8
SGU_GROUP_DIM = SGU_WIDTH // SGU_GROUPS
D_FF = 2816
N_MOD = 9
EPS = 1e-6
NEG_INF = -1e30


def rms_norm(x, g):
    x32 = x.astype(jnp.float32)
    y = x32 * lax.rsqrt(jnp.mean(x32 * x32, axis=-1, keepdims=True) + EPS)
    return (y * g.astype(jnp.float32)).astype(x.dtype)

def layer_norm(x, g, b):
    x32 = x.astype(jnp.float32)
    mu = jnp.mean(x32, axis=-1, keepdims=True)
    xc = x32 - mu
    y = xc * lax.rsqrt(jnp.mean(xc * xc, axis=-1, keepdims=True) + EPS)
    return (y * g.astype(jnp.float32) + b.astype(jnp.float32)).astype(x.dtype)

def modulate(h, shift, scale):
    return h * (1.0 + scale[:, None, :]) + shift[:, None, :]

def swiglu(h, wg, wu, wd):
    return (jax.nn.silu(h @ wg) * (h @ wu)) @ wd

def t5_bucket(rel):
    n = jnp.maximum(rel, 0)
    nf = jnp.maximum(n, 1).astype(jnp.float32)
    large = REL_MAX_EXACT + (jnp.log(nf / REL_MAX_EXACT) / math.log(REL_MAX_DIST / REL_MAX_EXACT)
                             * (REL_BUCKETS - REL_MAX_EXACT)).astype(jnp.int32)
    large = jnp.minimum(large, REL_BUCKETS - 1)
    return jnp.where(n < REL_MAX_EXACT, n, large)

def diff_attention(h, w_qkv, q_g, k_g, lq1, lk1, lq2, lk2, subln_g, w_o, rel_bias, lambda_init):
    B, S, _ = h.shape
    q, k, v = jnp.split(h @ w_qkv, 3, axis=-1)
    q = rms_norm(q.reshape(B, S, DA_HEADS, 2, DA_HEAD_DIM), q_g)
    k = rms_norm(k.reshape(B, S, DA_HEADS, 2, DA_HEAD_DIM), k_g)
    v32 = v.reshape(B, S, DA_HEADS, DA_V_DIM).astype(jnp.float32)
    k32 = k.astype(jnp.float32)
    f32 = jnp.float32
    lam = (jnp.exp(jnp.sum(lq1.astype(f32) * lk1.astype(f32)))
           - jnp.exp(jnp.sum(lq2.astype(f32) * lk2.astype(f32))) + lambda_init)
    scale = 1.0 / math.sqrt(DA_HEAD_DIM)
    nb = S // Q_BLOCK
    qb = q.reshape(B, nb, Q_BLOCK, DA_HEADS, 2, DA_HEAD_DIM).transpose(1, 0, 2, 3, 4, 5)
    k_pos = jnp.arange(S, dtype=jnp.int32)
    table = rel_bias.astype(f32)

    def block(args):
        q_blk, bi = args
        q_pos = bi * Q_BLOCK + jnp.arange(Q_BLOCK, dtype=jnp.int32)
        rel = q_pos[:, None] - k_pos[None, :]
        bias = jnp.where((rel >= 0)[..., None], table[t5_bucket(rel)], NEG_INF)
        bias = bias.transpose(2, 0, 1)
        logits = jnp.einsum('bqhcd,bkhcd->bhcqk', q_blk.astype(f32), k32) * scale + bias[None, :, None]
        p = jax.nn.softmax(logits, axis=-1)
        attn = p[:, :, 0] - lam * p[:, :, 1]
        o = jnp.einsum('bhqk,bkhe->bqhe', attn, v32)
        o = rms_norm(o, subln_g) * (1.0 - lambda_init)
        return o.reshape(B, Q_BLOCK, DA_HEADS * DA_V_DIM).astype(h.dtype)

    out = lax.map(block, (qb, jnp.arange(nb, dtype=jnp.int32)))
    out = out.transpose(1, 0, 2, 3).reshape(B, S, DA_HEADS * DA_V_DIM)
    return out @ w_o

def spatial_gating(h, w_in, ln_g, ln_b, w_s, b_s, w_out):
    B, S, _ = h.shape
    z = jax.nn.gelu(h @ w_in, approximate=False)
    u, v = jnp.split(z, 2, axis=-1)
    v = layer_norm(v, ln_g, ln_b)
    nc = S // SGU_CHUNK
    v = v.reshape(B, nc, SGU_CHUNK, SGU_GROUPS, SGU_GROUP_DIM)
    causal = jnp.tril(jnp.ones((SGU_CHUNK, SGU_CHUNK), dtype=w_s.dtype))
    mixed = jnp.einsum('gts,bnsgc->bntgc', w_s * causal, v) + b_s.T[:, :, None]
    gated = u * mixed.reshape(B, S, SGU_WIDTH)
    return gated @ w_out

def _normal(k, shape, std):
    return jax.random.normal(k, shape, jnp.float32) * std

def first_inputs(seed: int = 0) -> dict:
    key = jax.random.key(seed)
    ks = jax.random.split(key, 32)
    D, F = D_MODEL, D_FF
    gain = lambda k, shape: 1.0 + _normal(k, shape, 0.1)
    return {
        'x': _normal(ks[0], (BATCH, SEQ, D), 1.0),
        'c': _normal(ks[1], (BATCH, D), 1.0),
        'rel_bias': _normal(ks[2], (REL_BUCKETS, DA_HEADS), 0.5),
        'ada_w': _normal(ks[3], (DEPTH, D, N_MOD * D), 0.5 * D ** -0.5),
        'ada_b': _normal(ks[4], (DEPTH, N_MOD * D), 0.02),
        'ln_ffn1': gain(ks[5], (DEPTH, D)),
        'ffn1_wg': _normal(ks[6], (DEPTH, D, F), D ** -0.5),
        'ffn1_wu': _normal(ks[7], (DEPTH, D, F), D ** -0.5),
        'ffn1_wd': _normal(ks[8], (DEPTH, F, D), F ** -0.5),
        'ln_mix': gain(ks[9], (DEPTH, D)),
        'ln_ffn2': gain(ks[10], (DEPTH, D)),
        'ffn2_wg': _normal(ks[11], (DEPTH, D, F), D ** -0.5),
        'ffn2_wu': _normal(ks[12], (DEPTH, D, F), D ** -0.5),
        'ffn2_wd': _normal(ks[13], (DEPTH, F, D), F ** -0.5),
        'ln_out': gain(ks[14], (DEPTH, D)),
        'attn_w_qkv': _normal(ks[15], (N_A_LAYERS, D, 3 * D), D ** -0.5),
        'attn_q_norm': gain(ks[16], (N_A_LAYERS, DA_HEAD_DIM)),
        'attn_k_norm': gain(ks[17], (N_A_LAYERS, DA_HEAD_DIM)),
        'attn_lq1': _normal(ks[18], (N_A_LAYERS, DA_HEAD_DIM), 0.1),
        'attn_lk1': _normal(ks[19], (N_A_LAYERS, DA_HEAD_DIM), 0.1),
        'attn_lq2': _normal(ks[20], (N_A_LAYERS, DA_HEAD_DIM), 0.1),
        'attn_lk2': _normal(ks[21], (N_A_LAYERS, DA_HEAD_DIM), 0.1),
        'attn_subln': gain(ks[22], (N_A_LAYERS, DA_V_DIM)),
        'attn_w_o': _normal(ks[23], (N_A_LAYERS, D, D), D ** -0.5),
        'sgu_w_in': _normal(ks[24], (N_B_LAYERS, D, 2 * SGU_WIDTH), D ** -0.5),
        'sgu_ln_g': gain(ks[25], (N_B_LAYERS, SGU_WIDTH)),
        'sgu_ln_b': _normal(ks[26], (N_B_LAYERS, SGU_WIDTH), 0.02),
        'sgu_w_s': _normal(ks[27], (N_B_LAYERS, SGU_GROUPS, SGU_CHUNK, SGU_CHUNK), SGU_CHUNK ** -0.5),
        'sgu_b_s': gain(ks[28], (N_B_LAYERS, SGU_GROUPS, SGU_CHUNK)),
        'sgu_w_out': _normal(ks[29], (N_B_LAYERS, SGU_WIDTH, D), SGU_WIDTH ** -0.5),
    }

def first_block(x, c, rel_bias, ada_w, ada_b, ln_ffn1, ffn1_wg, ffn1_wu, ffn1_wd, ln_mix,
              ln_ffn2, ffn2_wg, ffn2_wu, ffn2_wd, ln_out, attn_w_qkv, attn_q_norm, attn_k_norm,
              attn_lq1, attn_lk1, attn_lq2, attn_lk2, attn_subln, attn_w_o, sgu_w_in, sgu_ln_g,
              sgu_ln_b, sgu_w_s, sgu_b_s, sgu_w_out):
    c_act = jax.nn.silu(c)
    for i in range(DEPTH):
        mod = c_act @ ada_w[i] + ada_b[i]
        sh1, sc1, g1, sh2, sc2, g2, sh3, sc3, g3 = jnp.split(mod, N_MOD, axis=-1)
        h = modulate(rms_norm(x, ln_ffn1[i]), sh1, sc1)
        x = x + 0.5 * g1[:, None, :] * swiglu(h, ffn1_wg[i], ffn1_wu[i], ffn1_wd[i])
        h = modulate(rms_norm(x, ln_mix[i]), sh2, sc2)
        j = i // N_MIXERS
        if i % N_MIXERS == 0:
            lambda_init = 0.8 - 0.6 * math.exp(-0.3 * i)
            mix = diff_attention(h, attn_w_qkv[j], attn_q_norm[j], attn_k_norm[j], attn_lq1[j],
                                 attn_lk1[j], attn_lq2[j], attn_lk2[j], attn_subln[j], attn_w_o[j],
                                 rel_bias, lambda_init)
        else:
            mix = spatial_gating(h, sgu_w_in[j], sgu_ln_g[j], sgu_ln_b[j], sgu_w_s[j], sgu_b_s[j],
                                 sgu_w_out[j])
        x = x + g2[:, None, :] * mix
        h = modulate(rms_norm(x, ln_ffn2[i]), sh3, sc3)
        x = x + 0.5 * g3[:, None, :] * swiglu(h, ffn2_wg[i], ffn2_wu[i], ffn2_wd[i])
        x = rms_norm(x, ln_out[i])
    return x


DEPTH_2 = 1

N_HGRN_LAYERS = (DEPTH_2 + N_MIXERS - 1) // N_MIXERS
N_ATTN_LAYERS = (DEPTH_2 - 1 + N_MIXERS - 1) // N_MIXERS

HGRN_HEAD_DIM = 128
HGRN_HEADS = D_MODEL // HGRN_HEAD_DIM
HGRN_CHUNK = 64

ATTN_HEADS = 16
ATTN_HEAD_DIM = D_MODEL // ATTN_HEADS
DILATED_GROUPS = ((128, 1), (512, 4), (2048, 16))
N_GROUPS = len(DILATED_GROUPS)
ATTN_BLOCK = 128

MLP_HIDDEN = 4 * D_MODEL
NORM_EPS = 1e-6


def _rmsnorm(x, gain):
    xf = x.astype(jnp.float32)
    y = xf * lax.rsqrt(jnp.mean(xf * xf, axis=-1, keepdims=True) + NORM_EPS)
    return (y * gain.astype(jnp.float32)).astype(x.dtype)

def _hgrn2_chunk_scan(q, k, v, log_f):
    b, s, h, dk = q.shape
    dv = v.shape[-1]
    nc = s // HGRN_CHUNK

    def to_chunks(t):
        return t.reshape(b, nc, HGRN_CHUNK, h, t.shape[-1]).transpose(1, 0, 3, 2, 4)

    causal = jnp.tril(jnp.ones((HGRN_CHUNK, HGRN_CHUNK), dtype=bool))

    def step(state, inp):
        qi, ki, vi, gi = inp
        cum = jnp.cumsum(gi, axis=2)
        o_inter = jnp.einsum('bhtk,bhkv->bhtv', qi * jnp.exp(cum), state)
        diff = cum[:, :, :, None, :] - cum[:, :, None, :, :]
        decay = jnp.exp(jnp.where(causal[:, :, None], diff, -jnp.inf))
        scores = jnp.einsum('bhtk,bhtsk,bhsk->bhts', qi, decay, ki)
        o_intra = jnp.einsum('bhts,bhsv->bhtv', scores, vi)
        last = cum[:, :, -1:, :]
        k_dec = ki * jnp.exp(last - cum)
        new_state = (jnp.exp(last[:, :, 0, :])[..., None] * state
                     + jnp.einsum('bhsk,bhsv->bhkv', k_dec, vi))
        return new_state, o_inter + o_intra

    init = jnp.zeros((b, h, dk, dv), jnp.float32)
    _, o = lax.scan(step, init, (to_chunks(q), to_chunks(k), to_chunks(v), to_chunks(log_f)))
    return o.transpose(1, 0, 3, 2, 4).reshape(b, s, h, dv)

def _hgrn2_mixer(h, w_in, lower_bound, out_norm, w_out):
    b, s, _ = h.shape
    proj = h @ w_in
    q, f, i, g = jnp.split(proj, 4, axis=-1)
    ff = f.astype(jnp.float32)
    lb = lower_bound.astype(jnp.float32)
    log_f = jnp.logaddexp(jnp.log(lb), jnp.log1p(-lb) + jax.nn.log_sigmoid(ff))
    k = (1.0 - lb) * jax.nn.sigmoid(-ff)
    qf = jax.nn.silu(q.astype(jnp.float32)) * (HGRN_HEAD_DIM ** -0.5)
    heads = lambda t: t.reshape(b, s, HGRN_HEADS, HGRN_HEAD_DIM)
    o = _hgrn2_chunk_scan(heads(qf), heads(k), heads(i.astype(jnp.float32)), heads(log_f))
    o = o * lax.rsqrt(jnp.mean(o * o, axis=-1, keepdims=True) + NORM_EPS)
    o = o.reshape(b, s, D_MODEL) * out_norm.astype(jnp.float32) * jax.nn.silu(g.astype(jnp.float32))
    return o.astype(h.dtype) @ w_out

def _banded_causal_attention(q, k, v, reach):
    n, l, h, dh = q.shape
    blk = ATTN_BLOCK
    nb = -(-l // blk)
    lp = nb * blk
    qb = jnp.pad(q, ((0, 0), (0, lp - l), (0, 0), (0, 0))).reshape(n, nb, blk, h, dh)
    pad_kv = ((0, 0), (blk, lp - l), (0, 0), (0, 0))
    kp = jnp.pad(k, pad_kv).reshape(n, nb + 1, blk, h, dh)
    vp = jnp.pad(v, pad_kv).reshape(n, nb + 1, blk, h, dh)
    kb = jnp.concatenate([kp[:, :-1], kp[:, 1:]], axis=2)
    vb = jnp.concatenate([vp[:, :-1], vp[:, 1:]], axis=2)
    bidx = jnp.arange(nb)[:, None, None]
    qpos = bidx * blk + jnp.arange(blk)[None, :, None]
    kpos = (bidx - 1) * blk + jnp.arange(2 * blk)[None, None, :]
    dist = qpos - kpos
    mask = (kpos >= 0) & (dist >= 0) & (dist <= reach)
    s = jnp.einsum('nbqhd,nbkhd->nbhqk', qb, kb).astype(jnp.float32) * (dh ** -0.5)
    s = jnp.where(mask[None, :, None], s, -jnp.inf)
    lse = jax.nn.logsumexp(s, axis=-1)
    p = jnp.exp(s - lse[..., None])
    o = jnp.einsum('nbhqk,nbkhd->nbqhd', p.astype(v.dtype), vb).astype(jnp.float32)
    o = o.reshape(n, lp, h, dh)[:, :l]
    lse = lse.transpose(0, 1, 3, 2).reshape(n, lp, h)[:, :l]
    return o, lse

def _dilated_group(q, k, v, dilation, reach):
    b, s, h, dh = q.shape
    l = s // dilation

    def split(t):
        return t.reshape(b, l, dilation, h, dh).transpose(0, 2, 1, 3, 4).reshape(b * dilation, l, h, dh)

    o, lse = _banded_causal_attention(split(q), split(k), split(v), reach)
    o = o.reshape(b, dilation, l, h, dh).transpose(0, 2, 1, 3, 4).reshape(b, s, h, dh)
    lse = lse.reshape(b, dilation, l, h).transpose(0, 2, 1, 3).reshape(b, s, h)
    return o, lse

def _dilated_attention_mixer(h, w_qkv, w_out):
    b, s, _ = h.shape
    proj = (h @ w_qkv).reshape(b, s, N_GROUPS, 3, ATTN_HEADS, ATTN_HEAD_DIM)
    outs, lses = [], []
    for g, (window, dilation) in enumerate(DILATED_GROUPS):
        o, lse = _dilated_group(proj[:, :, g, 0], proj[:, :, g, 1], proj[:, :, g, 2],
                                dilation, window // dilation)
        outs.append(o)
        lses.append(lse)
    weights = jax.nn.softmax(jnp.stack(lses, axis=0), axis=0)
    o = jnp.sum(weights[..., None] * jnp.stack(outs, axis=0), axis=0)
    return o.reshape(b, s, D_MODEL).astype(h.dtype) @ w_out

def _squared_relu_mlp(h, w1, w2):
    a = jax.nn.relu(h @ w1)
    return (a * a) @ w2

def second_inputs(seed: int = 0) -> dict:
    key = jax.random.key(seed)
    ks = jax.random.split(key, 13)
    nrm = lambda k, shape: jax.random.normal(k, shape, jnp.float32)
    d = D_MODEL
    return {
        "x": nrm(ks[0], (BATCH, SEQ, d)),
        "norm_mix": 1.0 + 0.02 * nrm(ks[1], (DEPTH_2, d)),
        "norm_mlp": 1.0 + 0.02 * nrm(ks[2], (DEPTH_2, d)),
        "norm_final": 1.0 + 0.02 * nrm(ks[3], (d,)),
        "hgrn_w_in": nrm(ks[4], (N_HGRN_LAYERS, d, 4 * d)) * d ** -0.5,
        "hgrn_lower_bound": 0.5 * nrm(ks[5], (N_HGRN_LAYERS, d)),
        "hgrn_out_norm": 1.0 + 0.02 * nrm(ks[6], (N_HGRN_LAYERS, d)),
        "hgrn_w_out": nrm(ks[7], (N_HGRN_LAYERS, d, d)) * d ** -0.5,
        "attn_w_qkv": nrm(ks[8], (N_ATTN_LAYERS, d, N_GROUPS * 3 * d)) * d ** -0.5,
        "attn_w_out": nrm(ks[9], (N_ATTN_LAYERS, d, d)) * d ** -0.5,
        "mlp_w1": nrm(ks[10], (DEPTH_2, d, MLP_HIDDEN)) * d ** -0.5,
        "mlp_w2": nrm(ks[11], (DEPTH_2, MLP_HIDDEN, d)) * MLP_HIDDEN ** -0.5,
    }

def second_block(x, norm_mix, norm_mlp, norm_final, hgrn_w_in, hgrn_lower_bound, hgrn_out_norm,
              hgrn_w_out, attn_w_qkv, attn_w_out, mlp_w1, mlp_w2):
    lb_all = jnp.cumsum(jax.nn.softmax(hgrn_lower_bound.astype(jnp.float32), axis=0), axis=0)
    lb_all = lb_all - lb_all[0]
    for layer in range(DEPTH_2):
        j = layer // N_MIXERS
        h = _rmsnorm(x, norm_mix[layer])
        if layer % N_MIXERS == 0:
            mix = _hgrn2_mixer(h, hgrn_w_in[j], lb_all[j], hgrn_out_norm[j], hgrn_w_out[j])
        else:
            mix = _dilated_attention_mixer(h, attn_w_qkv[j], attn_w_out[j])
        x = x + mix
        x = x + _squared_relu_mlp(_rmsnorm(x, norm_mlp[layer]), mlp_w1[layer], mlp_w2[layer])
    return _rmsnorm(x, norm_final)


def setup_inputs(seed=0):
    out = dict(first_inputs(seed))
    for name, value in second_inputs(seed + 1).items():
        if name != "x":
            out[name + "_2"] = value
    return out


def reference(
    x, c, rel_bias, ada_w, ada_b, ln_ffn1, ffn1_wg, ffn1_wu, ffn1_wd, ln_mix, ln_ffn2, ffn2_wg,
    ffn2_wu, ffn2_wd, ln_out, attn_w_qkv, attn_q_norm, attn_k_norm, attn_lq1, attn_lk1,
    attn_lq2, attn_lk2, attn_subln, attn_w_o, sgu_w_in, sgu_ln_g, sgu_ln_b, sgu_w_s, sgu_b_s,
    sgu_w_out, norm_mix_2, norm_mlp_2, norm_final_2, hgrn_w_in_2, hgrn_lower_bound_2,
    hgrn_out_norm_2, hgrn_w_out_2, attn_w_qkv_2, attn_w_out_2, mlp_w1_2, mlp_w2_2,
):
    x = first_block(
        x, c, rel_bias, ada_w, ada_b, ln_ffn1, ffn1_wg, ffn1_wu, ffn1_wd, ln_mix, ln_ffn2,
        ffn2_wg, ffn2_wu, ffn2_wd, ln_out, attn_w_qkv, attn_q_norm, attn_k_norm, attn_lq1,
        attn_lk1, attn_lq2, attn_lk2, attn_subln, attn_w_o, sgu_w_in, sgu_ln_g, sgu_ln_b,
        sgu_w_s, sgu_b_s, sgu_w_out,
    )
    return second_block(
        x, norm_mix_2, norm_mlp_2, norm_final_2, hgrn_w_in_2, hgrn_lower_bound_2,
        hgrn_out_norm_2, hgrn_w_out_2, attn_w_qkv_2, attn_w_out_2, mlp_w1_2, mlp_w2_2,
    )


_drawn_inputs = setup_inputs


def setup_inputs(seed=0):
    import zlib

    import numpy as np

    out = dict(_drawn_inputs(seed))
    spreads = {}
    factors = {'attn_q_norm': 3.355,
     'attn_k_norm': 4.014,
     'attn_lq2': 7.506,
     'attn_lk2': 5.257,
     'sgu_ln_g': 2.996,
     'sgu_ln_b': 8.0,
     'norm_mix_2': 3.493,
     'norm_mlp_2': 11.484,
     'norm_final_2': 8.091,
     'hgrn_out_norm_2': 14.789}
    for name, (base, spread) in spreads.items():
        noise = np.random.default_rng([zlib.crc32(name.encode()), seed]).standard_normal(out[name].shape)
        drawn = base * np.exp(spread * noise) if base else spread * noise
        out[name] = __import__('jax').numpy.asarray(drawn.astype(out[name].dtype))
    for name, factor in factors.items():
        out[name] = (out[name] * factor).astype(out[name].dtype)
    return out
```

```python
import math
from contextlib import ExitStack

import numpy as np

import concourse.bass as bass
from concourse import mybir

F32 = mybir.dt.float32
F32R = mybir.dt.float32r
I32 = mybir.dt.int32
ACT = mybir.ActivationFunctionType
ALU = mybir.AluOpType

P = 128
D = 1024
S = 512
DB = D // P
TB = S // P
FF = 2816
HID = 4096
N_MOD = 9
MODB = N_MOD * DB
TW = 256
KB = 8
HEADS = 8
EPS = 1e-6
BUCKETS = 32
STRIP = S + P
NEG = -1e30
LEVELS = 7
Q_SCALE = 0.125
H_SCALE = 128 ** -0.5
LAMBDA_INIT = 0.8 - 0.6 * math.exp(-0.3 * 0)

V_ADA = (0, 128)
V_C = 72
V_LN = 256
V_NORM2 = V_LN + 64
V_LB = V_NORM2 + 24
V_ON = V_LB + 8
V_SUB = V_ON + 8
V_COLS = V_SUB + 1


def shape_constants():
    s, t = np.meshgrid(np.arange(P), np.arange(P), indexing="ij")
    pats = [s == t, (s // 64) == (t // 64)]
    for lv in range(LEVELS):
        h = 1 << lv
        pats.append((s // (2 * h) == t // (2 * h)) & (s % (2 * h) < h) & (t % (2 * h) >= h))
    pats.append(s <= t)
    consts = np.concatenate([p.astype(np.float32) for p in pats], axis=1)
    rel = (S - 1) - np.arange(STRIP)
    n = np.maximum(rel, 1).astype(np.float32)
    exact = BUCKETS // 2
    large = exact + (np.log(n / np.float32(exact)) / np.float32(math.log(128 / exact)) * np.float32(exact)).astype(np.int32)
    bucket = np.where(rel < exact, rel, np.minimum(large, BUCKETS - 1))
    bucket = np.where(rel < 0, BUCKETS, bucket)
    onehot = (np.arange(BUCKETS + 1)[:, None] == bucket[None, :]).astype(np.float32)
    return consts, onehot


C_IDENT, C_BLK64, C_MASK, C_CAUSAL = 0, 1, 2, 2 + LEVELS


class Op:

    def __init__(self, kind, wg=None, wu=None, w=None, layer=0, col=0, row=0, nb=0, kb=KB, ada=0, gate=None,
                 gain=None, shift=None, last=False):
        self.kind, self.wg, self.wu, self.w, self.layer = kind, wg, wu, w, layer
        self.col, self.row, self.nb, self.kb, self.ada = col, row, nb, kb, ada
        self.gate, self.gain, self.shift, self.last = gate, gain, shift, last


def make_plan():
    ops = []

    def ffn(layer, which, gate, ada):
        k0 = 0
        for g, nb in enumerate((8, 8, 6)):
            ops.append(Op("up", wg=f"{which}_wg", wu=f"{which}_wu", layer=layer, col=k0, nb=nb,
                          ada=ada[g] if ada else 0))
            if ada:
                ops.append(Op("adafin", layer=ada[3]))
            ops.append(Op("down", w=f"{which}_wd", layer=layer, row=k0, kb=nb, gate=(layer, gate), last=g == 2))
            k0 += nb * P

    def norm(layer, i):
        ops.append(Op("norm", gain=("gain", layer, i), shift=(layer, i)))

    for layer in range(2):
        norm(layer, 0)
        if layer == 0:
            ops.append(Op("ada4"))
            ops.append(Op("adafin", layer=0))
        ffn(layer, "ffn1", 0, (4, 2, 0, 0) if layer == 0 else None)
        norm(layer, 1)
        if layer == 0:
            ops.append(Op("attn"))
            ops.append(Op("down", w="attn_w_o", layer=0, row=0, kb=8, gate=(layer, 1), last=True))
        else:
            ops.append(Op("sgu"))
            ops.append(Op("down", w="sgu_w_out", layer=0, row=0, kb=8, gate=(layer, 1), last=True))
        norm(layer, 2)
        ffn(layer, "ffn2", 2, (4, 2, 4, 1) if layer == 0 else None)
        ops.append(Op("renorm", gain=("vec", V_LN + 48 + 8 * layer)))
    ops.append(Op("norm", gain=("vec", V_NORM2), shift=None))
    ops.append(Op("hgrn"))
    ops.append(Op("down", w="hgrn_w_out_2", layer=0, row=0, kb=8, gate=None, last=True))
    ops.append(Op("norm", gain=("vec", V_NORM2 + 8), shift=None))
    for g in range(4):
        ops.append(Op("upsq", w="mlp_w1_2", layer=0, col=g * D))
        ops.append(Op("down", w="mlp_w2_2", layer=0, row=g * D, kb=8, gate=None, last=g == 3))
    ops.append(Op("final", gain=("vec", V_NORM2 + 16)))

    t = x = n = h = v = a = c = 0
    x, c, fin = 8, 8, 1
    batch = [0, 8]
    for op in ops:
        op.t0, op.x0, op.n0, op.h0, op.v0, op.a0, op.c0 = t, x, n, h, v, a, c
        if op.kind == "up":
            t += op.nb
            v += op.nb
            a += op.nb
            c += op.ada * (op.nb // 2)
        elif op.kind == "ada4":
            c += 4
        elif op.kind == "adafin":
            op.cb, op.ce, op.fin = batch[1], c, fin + 1
            op.skip = op.ce == op.cb
            if not op.skip:
                fin += 1
                batch = [op.cb, c]
                op.m0, op.m1 = 2 * (op.cb - 36 * op.layer), 2 * (op.ce - 36 * op.layer)
        elif op.kind == "upsq":
            t += 4
            v += 8
            a += 8
        elif op.kind == "down":
            t += 4
            x += 8
        elif op.kind in ("norm", "final"):
            n += 1
            h += op.kind == "norm"
        elif op.kind == "renorm":
            n += 1
            x += 8
        elif op.kind == "attn":
            t += 12
            a += 8
        elif op.kind == "sgu":
            t += 8
            a += 8
        elif op.kind == "hgrn":
            t += 16
            a += 8
    return ops, t


def attn_sequence():
    seq = [("blk", 0, m) for m in range(4)]
    for j in range(1, 4):
        for m in range(4):
            seq.append(("blk", j, m))
            seq += [("row", 8 * (j - 1) + 2 * m), ("row", 8 * (j - 1) + 2 * m + 1)]
    seq += [("row", n) for n in range(24, 32)]
    return seq


HG_UNITS = [("g", 0), ("g", 1), ("i", 0), ("i", 1), ("f", 0), ("f", 1), ("q", 0), ("q", 1)]
HG_STEPS = LEVELS + 1 + 2 + 1


def hgrn_sequence():
    seq = [("unit", 0, u) for u in range(8)]
    for j in range(1, 4):
        steps = [("step", 2 * (j - 1) + s // HG_STEPS, s % HG_STEPS) for s in range(2 * HG_STEPS)]
        for u in range(8):
            seq.append(("unit", j, u))
            a, b = len(steps) * u // 8, len(steps) * (u + 1) // 8
            seq += steps[a:b]
    seq += [("step", hd, s) for hd in (6, 7) for s in range(HG_STEPS)]
    return seq


def build_program(nc, ins, out):
    ops, T = make_plan()
    with ExitStack() as ctx:
        def sb(name, shape, dt=F32):
            return ctx.enter_context(nc.sbuf_tensor(name, shape, dt))

        def sem(name):
            return ctx.enter_context(nc.semaphore(name))

        x = sb("x", [P, DB * S])
        h_hi = sb("h_hi", [P, DB * S], F32R)
        h_lo = sb("h_lo", [P, DB * S], F32R)
        a_hi_t = sb("act_hi", [P, DB * S], F32R)
        a_lo_t = sb("act_lo", [P, DB * S], F32R)
        w_raw = sb("w_raw", [P, 2, KB, TW])
        w_hi_t = sb("w_hi_t", [P, 2, KB, TW], F32R)
        w_lo_t = sb("w_lo_t", [P, 2, KB, TW], F32R)
        scr = sb("scr", [P, 12288])
        hidden = sb("hidden", [P, 8 * S])
        sq = sb("sq", [P, 2, S])
        ssq = sb("ssq", [P, S])
        rstd = sb("rstd", [P, S])
        ident = sb("ident", [P, P])
        blk64 = sb("blk64", [P, P])
        ones = sb("ones", [P, P])
        vec = sb("vec", [P, V_COLS])
        mod = sb("mod", [P, 2, MODB])
        gain = sb("gain", [P, 2, 3, DB])
        half = sb("half", [P, 2, 2, DB])
        cact = sb("cact", [P, DB])
        small = sb("small", [P, 64])
        eps = small[:, 0:1]
        qk_gain = small[:, 1:3]
        sub_gain = small[:, 3:4]
        neg_lam = small[:, 4:5]
        one_lb = small[:, 8:16]
        lb = small[:, 16:24]
        stat = small[:, 24:64]

        ps = [ctx.enter_context(nc.psum_tensor(f"bank{i}", [P, S], F32)) for i in range(8)]

        bias_rows = nc.dram_tensor("bias_rows", (HEADS, STRIP), F32).ap()
        bias_rep = nc.dram_tensor("bias_rep", (HEADS, P, STRIP), F32).ap()

        ada_acc = scr[:, 0:4096]
        ada_raw = scr[:, 4096:8192].rearrange("p (s k n) -> p s k n", s=2, k=KB)
        x_nat = scr[:, 8192:12288].rearrange("p (t d) -> p t d", t=TB)
        vrow = hidden[:, 0:384].rearrange("p (g n) -> p g n", g=3)
        at_v = scr[:, 0:4096].rearrange("p (t d) -> p t d", t=TB)
        at_bias = scr[:, 4096:8192].rearrange("p (h u) -> p h u", h=HEADS)
        at_qk = scr[:, 8192:12288].rearrange("p (b c h t) -> p b c h t", b=2, c=2, h=2)
        at_tr = hidden[:, 0:2048].rearrange("p (k t) -> p k t", k=TB)
        at_s = hidden[:, 2048:4096].rearrange("p (b c t) -> p b c t", b=2, c=2)
        sg_v = scr[:, 0:4096].rearrange("p (t d) -> p t d", t=TB)
        sg_u = scr[:, 4096:8192]
        sg_ws = scr[:, 8192:9216].rearrange("p (g t) -> p g t", g=8)
        sg_bs = scr[:, 9216:10240]
        sg_g = scr[:, 10240:11264]
        sg_b = scr[:, 11264:12288]
        sg_wn = hidden[:, 0:1024].rearrange("p (g t) -> p g t", g=8)
        sg_mask = hidden[:, 1024:1152]
        hg_v = scr[:, 0:2048].rearrange("p (b t n) -> p b t n", b=2, t=TB)
        hg_g = scr[:, 2048:4096].rearrange("p (b h t) -> p b h t", b=2, h=2)
        hg_f = scr[:, 4096:6144].rearrange("p (b h t) -> p b h t", b=2, h=2)
        hg_k = scr[:, 6144:8192].rearrange("p (b h t) -> p b h t", b=2, h=2)
        hg_q = scr[:, 8192:10240].rearrange("p (b h t) -> p b h t", b=2, h=2)
        hg_l = scr[:, 10240:10752]
        hg_mask = scr[:, 10752:11648].rearrange("p (l t) -> p l t", l=LEVELS)
        hg_p = hidden[:, 0:2048]
        hg_qe = hidden[:, 2048:3072].rearrange("p (b t) -> p b t", b=2)
        hg_ke = hidden[:, 3072:4096].rearrange("p (b t) -> p b t", b=2)

        raw_in = [sem("raw_in0"), sem("raw_in1")]
        w_hi = sem("w_hi")
        w_lo = sem("w_lo")
        blk_mm = sem("blk_mm")
        ada_in = [sem("ada_in0"), sem("ada_in1")]
        ada_ch = sem("ada_ch")
        ada_mm = sem("ada_mm")
        mod_ok = sem("mod_ok")
        cst_in = sem("cst_in")
        xin = sem("xin")
        bias_d = sem("bias_d")
        bias_sb = sem("bias_sb")
        init_d = sem("init_d")
        init_p = sem("init_p")
        init_a = sem("init_a")
        x_upd = sem("x_upd")
        sq_done = sem("sq_done")
        ssq_done = sem("ssq_done")
        ssum_mm = sem("ssum_mm")
        root_ok = sem("root_ok")
        h_t = sem("h_t")
        h_hi_s = sem("h_hi_s")
        h_lo_s = sem("h_lo_s")
        act1 = sem("act1")
        v_done = sem("v_done")
        a_hi_s = sem("a_hi_s")
        a_lo_s = sem("a_lo_s")
        chain = sem("chain")
        mix_d = sem("mix_d")
        nat_ev = sem("nat_ev")
        qsq = sem("qsq")
        qss = sem("qss")
        qroot = sem("qroot")
        qk_ok = sem("qk_ok")
        s_mm = sem("s_mm")
        s_rd = sem("s_rd")
        mx_ok = sem("mx_ok")
        exp_ok = sem("exp_ok")
        at_ok = sem("at_ok")
        t_mm = sem("t_mm")
        t_ev = sem("t_ev")
        o_mm = sem("o_mm")
        o_sq = sem("o_sq")
        o_ss = sem("o_ss")
        o_root = sem("o_root")
        o_ok = sem("o_ok")
        sg_st = sem("sg_st")
        sg_rt = sem("sg_rt")
        sg_vn = sem("sg_vn")
        sg_tr = sem("sg_tr")
        sg_wm = sem("sg_wm")
        sg_mm = sem("sg_mm")
        sg_ev = sem("sg_ev")
        sg_ge = sem("sg_ge")
        sg_go = sem("sg_go")
        hg_ev = sem("hg_ev")
        hg_in = sem("hg_in")
        hg_qk = sem("hg_qk")
        hg_mm = sem("hg_mm")
        hg_pc = sem("hg_pc")
        hg_far = sem("hg_far")
        fin_t = sem("fin_t")
        fin_c = sem("fin_c")
        out_d = sem("out_d")

        def gain_col(op, kb):
            g = op.gain
            return gain[:, g[1], g[2], kb:kb + 1] if g[0] == "gain" else vec[:, g[1] + kb:g[1] + kb + 1]

        def shift_col(op, kb):
            layer, i = op.shift
            m = 3 * i * DB + kb
            return mod[:, layer, m:m + 1]

        def gate_col(op, nb):
            layer, i = op.gate
            if i == 1:
                m = 5 * DB + nb
                return mod[:, layer, m:m + 1]
            return half[:, layer, i // 2, nb:nb + 1]

        def blk(t, n):
            return t[:, bass.ds(n * S, S)] if not isinstance(n, int) else t[:, n * S:(n + 1) * S]

        def bcast(ap, dims):
            return bass.AP(tensor=ap.tensor, offset=ap.offset, ap=[list(ap.ap[0])] + dims)

        def tile_src(name, layer, row, kb):
            w = ins[name][layer]
            return w[row:row + kb * P, :].rearrange("(k p) n -> p k n", p=P)

        n_tiles = T
        block = ctx.enter_context(nc.Block())

        @block.sync
        def _(sp):
            def weight(slot, t, src, kb=KB, skip_wait=False):
                if not skip_wait:
                    sp.wait_ge(w_lo, t - 1)
                sp.dma_start(w_raw[:, slot, 0:kb, :], src).then_inc(raw_in[slot], 16)

            def ada_chunk(slot, c, layer, col, skip_wait=False):
                if not skip_wait:
                    sp.wait_ge(ada_ch, 8 * (c - 1))
                src = ins["ada_w"][layer].rearrange("(k p) n -> p k n", p=P)
                sp.dma_start(ada_raw[:, slot], src[:, :, col]).then_inc(ada_in[slot], 16)

            rows = [("ada_b", 0, 0, 0, 72), ("c", 0, 0, V_C, 8), ("ada_b", 1, 1, 0, 72)]
            r = 0
            for name in ("ln_ffn1", "ln_mix", "ln_ffn2", "ln_out"):
                for layer in range(2):
                    rows.append((name, layer, 2, r, 8))
                    r += 8
            for name in ("norm_mix_2", "norm_mlp_2", "norm_final_2", "hgrn_lower_bound_2", "hgrn_out_norm_2"):
                rows.append((name, None if name == "norm_final_2" else 0, 2, r, 8))
                r += 8
            rows.append(("attn_subln", 0, 2, r, 1))
            for name, layer, grp, r0, n in rows:
                src = ins[name] if layer is None else ins[name][layer]
                sp.dma_start(vrow[r0:r0 + n, grp, :], src.rearrange("(r n) -> r n", n=P)).then_inc(cst_in, 16)
            sp.dma_start(ident[:], ins["consts"][:, 0:P]).then_inc(cst_in, 16)
            sp.dma_start(blk64[:], ins["consts"][:, P:2 * P]).then_inc(cst_in, 16)
            for c in range(2):
                ada_chunk(c, c, 0, slice(c * TW, (c + 1) * TW), True)
            sp.dma_start(x_nat, ins["x"][0].rearrange("(t p) d -> p t d", p=P)).then_inc(xin, 16)
            for i, name in enumerate(("attn_q_norm", "attn_k_norm")):
                for comp in range(2):
                    sp.dma_start(qk_gain[64 * comp:64 * comp + 64, i:i + 1],
                                 ins[name][0].rearrange("(p n) -> p n", n=1)).then_inc(xin, 16)
            for i, name in enumerate(("attn_lq1", "attn_lk1", "attn_lq2", "attn_lk2")):
                src = bass.AP(tensor=ins[name].tensor, offset=0, ap=[[0, P], [1, 64]])
                sp.dma_start(hidden[:, 512 + 64 * i:576 + 64 * i], src).then_inc(xin, 16)
            sp.dma_start(hidden[0:BUCKETS, 768:776], ins["rel_bias"]).then_inc(xin, 16)
            sp.dma_start(hidden[0:BUCKETS + 1, 1024:1024 + STRIP], ins["onehot"]).then_inc(xin, 16)
            for c in range(2, 8):
                ada_chunk(c % 2, c, 0, slice(c * TW, (c + 1) * TW))
            for slot, name in enumerate(("ffn1_wg", "ffn1_wu")):
                weight(slot, slot, tile_src(name, 0, 0, KB)[:, :, 0:TW], skip_wait=True)

            for op in ops:
                if op.kind == "ada4":
                    sp.wait_ge(bias_sb, 2)
                    sp.dma_start(bias_rows, hidden[0:HEADS, 2048:2048 + STRIP]).then_inc(bias_d, 16)
                    sp.wait_ge(bias_d, 16)
                    for hd in range(HEADS):
                        src = bass.AP(tensor=bias_rows.tensor, offset=hd * STRIP, ap=[[0, P], [1, STRIP]])
                        sp.dma_start(bias_rep[hd], src).then_inc(bias_d, 16)
                    for c in range(8, 12):
                        ada_chunk(c % 2, c, 0, slice(c * TW, (c + 1) * TW))
                elif op.kind == "up":
                    wg = tile_src(op.wg, op.layer, 0, KB)
                    wu = tile_src(op.wu, op.layer, 0, KB)
                    first = op.t0 == 0
                    a_layer = 0 if op.c0 < 36 else 1
                    if op.ada and op.c0 == 36:
                        sp.wait_ge(x_upd, op.x0)
                    if first:
                        for m in range(op.ada):
                            ada_chunk(m % 2, op.c0 + m, 0, slice((op.c0 + m) * TW, (op.c0 + m + 1) * TW))
                    with sp.Fori(1 if first else 0, op.nb // 2) as i:
                        weight(0, op.t0 + 2 * i, wg[:, :, bass.ds(i * TW + op.col, TW)])
                        weight(1, op.t0 + 2 * i + 1, wu[:, :, bass.ds(i * TW + op.col, TW)])
                        for m in range(op.ada):
                            c = op.ada * i + (op.c0 + m)
                            ada_chunk(m % 2, c, a_layer,
                                      bass.ds(i * (op.ada * TW) + (op.c0 + m - 36 * a_layer) * TW, TW))
                elif op.kind in ("down", "upsq"):
                    kb = op.kb if op.kind == "down" else KB
                    row = op.row if op.kind == "down" else 0
                    col = op.col if op.kind == "upsq" else 0
                    w = tile_src(op.w, op.layer, row, kb)
                    with sp.Fori(0, 2) as i:
                        for s in range(2):
                            weight(s, op.t0 + 2 * i + s, w[:, :, bass.ds(i * 2 * TW + (col + s * TW), TW)], kb)
                elif op.kind == "attn":
                    w = tile_src("attn_w_qkv", 0, 0, KB)
                    with sp.Fori(0, 2) as i:
                        for s in range(2):
                            weight(s, op.t0 + 2 * i + s, w[:, :, bass.ds(i * 2 * TW + (2 * D + s * TW), TW)])
                    sp.wait_ge(x_upd, op.x0)
                    sp.wait_ge(bias_d, 16 * (1 + HEADS))
                    for hd in range(HEADS):
                        src = bass.AP(tensor=bias_rep.tensor, offset=hd * P * STRIP + P - 1, ap=[[STRIP - 1, P], [1, S]])
                        sp.dma_start(at_bias[:, hd, :], src).then_inc(bias_d, 16)
                    with sp.Fori(0, 4) as i:
                        for s in range(2):
                            weight(s, op.t0 + 4 + 2 * i + s, w[:, :, bass.ds(i * TW + s * D, TW)])
                elif op.kind == "sgu":
                    w = tile_src("sgu_w_in", 0, 0, KB)
                    for base, col in ((0, D), (4, 0)):
                        with sp.Fori(0, 2) as i:
                            for s in range(2):
                                weight(s, op.t0 + base + 2 * i + s,
                                       w[:, :, bass.ds(i * 2 * TW + (col + s * TW), TW)])
                elif op.kind == "hgrn":
                    w = tile_src("hgrn_w_in_2", 0, 0, KB)
                    with sp.Fori(1, 5) as i:
                        for s, col in enumerate((3 * D, 2 * D, D, 0)):
                            weight(s % 2, op.t0 + 4 * i + (s - 4), w[:, :, bass.ds(i * TW + (col - TW), TW)])
                elif op.kind == "final":
                    for tb in range(TB):
                        sp.wait_ge(fin_c, 2 * tb + 2)
                        sp.dma_start(out[0, tb * P:(tb + 1) * P, :], at_v[:, tb, :]).then_inc(out_d, 16)
                    sp.wait_ge(out_d, 16 * TB)

        @block.gpsimd
        def _(pool):
            with pool.Fori(0, n_tiles // 2) as i:
                for s in range(2):
                    pool.wait_ge(w_hi, 2 * i + s + 1)
                    nc.gpsimd.tensor_tensor(w_lo_t[:, s], w_raw[:, s], w_hi_t[:, s].bitcast(F32),
                                            ALU.subtract).then_inc(w_lo, 1)

        def natural_out(act, op, dst, func, conv):
            for t in range(4):
                for tb in range(TB):
                    act.wait_ge(blk_mm, 2 * (op.t0 + t) + tb // 2 + 1)
                    act.activation(dst[:, tb, t * TW:(t + 1) * TW], ps[tb + 4 * (t % 2)][:, 0:TW], func)\
                       .then_inc(nat_ev, 1)
                conv(t % 2, op.t0 + 2 + t)

        def attn_turn(act, n):
            i = n % 4
            act.wait_ge(t_mm, n + 1)
            if i == 0 and n:
                act.wait_ge(o_mm, n // 4)
            src = ps[7][:, 0:(i + 1) * P].rearrange("p (k t) -> p k t", t=P)
            act.activation(at_tr[:, 0:i + 1, i * P:(i + 1) * P], src, ACT.Copy).then_inc(t_ev, 1)

        def attn_act(act, op, conv):
            def head_square(hd):
                act.wait_ge(o_mm, hd + 1)
                if hd:
                    act.wait_ge(o_ss, hd)
                act.activation(ssq[:], ps[6][:], ACT.Square).then_inc(o_sq, 1)

            def head_root(hd):
                act.wait_ge(o_ss, hd + 1)
                act.activation(rstd[:], ps[7][:], ACT.Sqrt, bias=eps, scale=1.0 / P).then_inc(o_root, 1)
                act.wait_ge(o_ok, hd + 1)
                act.copy(blk(a_hi_t, hd), sq[:, 1, :]).then_inc(a_hi_s, 1)

            for step in attn_sequence():
                if step[0] == "blk":
                    _, j, m = step
                    t = op.t0 + 4 + 2 * j + m // 2
                    n = 4 * j + m
                    act.wait_ge(blk_mm, 2 * t + m % 2 + 1)
                    if n:
                        act.wait_ge(qk_ok, n)
                    act.activation(sq[:, 0, :], ps[m][:], ACT.Square).then_inc(qsq, 1)
                    act.wait_ge(qss, n + 1)
                    act.activation(rstd[:], ps[6][:], ACT.Sqrt, bias=eps, scale=1.0 / 64).then_inc(qroot, 1)
                    if m % 2 == 1:
                        conv(m // 2, t + 2)
                else:
                    n = step[1]
                    par, K = n % 2, (n % 4 + 1) * P
                    act.wait_ge(mx_ok, n + 1)
                    for comp in range(2):
                        s = at_s[:, par, comp, 0:K]
                        ins_ = act.activation(s, s, ACT.Exp, bias=stat[:, 8 * par + 2 + comp:8 * par + 3 + comp],
                                              accum_out=stat[:, 8 * par + 4 + comp:8 * par + 5 + comp])
                        ins_.then_inc(exp_ok, 1)
                    if n >= 1:
                        attn_turn(act, n - 1)
                    if n >= 4 and n % 4 == 0:
                        head_square(n // 4 - 1)
                        head_root(n // 4 - 1)
            attn_turn(act, 31)
            head_square(7)
            head_root(7)

        def hgrn_act(act, op, conv):
            act.dma_start(hg_mask, ins["consts"][:, C_MASK * P:(C_MASK + LEVELS) * P]
                          .rearrange("p (l t) -> p l t", t=P)).then_inc(mix_d, 16)
            for step in hgrn_sequence():
                if step[0] == "unit":
                    _, j, u = step
                    kind, b = HG_UNITS[u]
                    t = op.t0 + 4 * j + u // 2
                    par = j % 2
                    act.wait_ge(blk_mm, 2 * t + b + 1)
                    if j >= 2 and u == 0:
                        act.wait_ge(a_lo_s, op.a0 + 2 * (j - 1))
                    if kind == "g":
                        act.activation(hg_g[:, par, b, :], ps[b][:], ACT.Silu).then_inc(hg_ev, 1)
                    elif kind == "i":
                        for tb in (2 * b, 2 * b + 1):
                            ins_ = act.activation(hg_v[:, par, tb, :], ps[tb][:, 0:TW], ACT.Copy)
                        ins_.then_inc(hg_ev, 1)
                    elif kind == "f":
                        act.activation(hg_f[:, par, b, :], ps[b][:], ACT.Sigmoid)
                        act.activation(hg_k[:, par, b, :], ps[b][:], ACT.Sigmoid, scale=-1.0).then_inc(hg_ev, 1)
                    else:
                        act.activation(hg_q[:, par, b, :], ps[2 + b][:], ACT.Silu).then_inc(hg_ev, 1)
                    if u % 2 == 1:
                        conv((u // 2) % 2, t + 2)
                else:
                    _, hd, s = step
                    n = hd * (LEVELS + 3) + s
                    if s in (LEVELS + 1, LEVELS + 2):
                        act.wait_ge(hg_mm, n + 1)
                        if s == LEVELS + 1:
                            src = ps[6][:, 0:2 * P].rearrange("p (a t) -> p a t", t=P)
                            dst = bcast(hg_p[:, P:2 * P], [[2 * S + 2 * P, 2], [1, P]])
                        else:
                            src = ps[7][:].rearrange("p (a t) -> p a t", t=2 * P)
                            dst = bcast(hg_p[:, 2 * P:4 * P], [[S, 2], [1, 2 * P]])
                        act.activation(dst, src, ACT.Copy).then_inc(hg_far, 1)
                    elif s == LEVELS + 3:
                        act.wait_ge(o_mm, 8 + hd + 1)
                        act.activation(ssq[:], ps[6][:], ACT.Square).then_inc(o_sq, 1)
                        act.wait_ge(o_ss, 8 + hd + 1)
                        act.activation(rstd[:], ps[7][:], ACT.Sqrt, bias=eps, scale=1.0 / P).then_inc(o_root, 1)
                        act.wait_ge(o_ok, 8 + hd + 1)
                        act.copy(blk(a_hi_t, hd), sq[:, 1, :]).then_inc(a_hi_s, 1)

        @block.scalar
        def _(act):
            def conv(slot, t):
                if isinstance(t, int):
                    if t >= n_tiles:
                        return
                    if t >= 2:
                        act.wait_ge(blk_mm, 2 * (t - 1))
                    act.wait_ge(raw_in[slot], 16 * (t // 2 + 1))
                    act.copy(w_hi_t[:, slot], w_raw[:, slot]).then_inc(w_hi, 1)

            def conv_at(slot, t0, i, step):
                act.wait_ge(blk_mm, 2 * step * i + 2 * (t0 - 1))
                act.wait_ge(raw_in[slot], 8 * step * i + 16 * (t0 // 2 + 1))
                act.copy(w_hi_t[:, slot], w_raw[:, slot]).then_inc(w_hi, 1)

            def square(n, kb, x_count):
                k = 8 * n + kb
                act.wait_ge(x_upd, x_count)
                if k >= 2:
                    act.wait_ge(ssq_done, k - 1)
                act.activation(sq[:, kb % 2, :], blk(x, kb), ACT.Square).then_inc(sq_done, 1)

            def root(n):
                act.wait_ge(ssum_mm, n + 1)
                act.activation(rstd[:], ps[6][:], ACT.Sqrt, bias=eps, scale=1.0 / D).then_inc(root_ok, 1)

            act.wait_ge(init_d, 3)
            act.activation(cact[:], vec[:, V_C:V_C + DB], ACT.Silu).then_inc(init_a, 1)
            act.wait_ge(init_d, 4)
            act.activation(small[:, 6:8], small[:, 6:8], ACT.Exp).then_inc(init_a, 1)
            for kb in range(DB):
                square(0, kb, kb + 1)
            act.wait_ge(bias_d, 16)
            for op in ops:
                nxt = op.t0 + 2
                if op.kind == "norm":
                    root(op.n0)
                    for kb in range(DB):
                        act.wait_ge(h_t, DB * op.h0 + kb + 1)
                        src = sq[:, kb % 2, :]
                        if op.shift:
                            act.activation(blk(h_hi, kb), src, ACT.Identity, bias=shift_col(op, kb),
                                           scale=gain_col(op, kb)).then_inc(h_hi_s, 1)
                        else:
                            act.copy(blk(h_hi, kb), src).then_inc(h_hi_s, 1)
                elif op.kind == "ada4":
                    conv(0, 0)
                    conv(1, 1)
                elif op.kind == "up":
                    with act.Fori(0, op.nb // 2) as i:
                        conv_at(0, nxt, i, 2)
                        for b in range(2):
                            act.wait_ge(blk_mm, 4 * i + (2 * (op.t0 + 1) + b + 1))
                            act.activation(blk(hidden, 2 * i + b), ps[b][:], ACT.Silu).then_inc(act1, 1)
                        for b in range(2):
                            act.wait_ge(v_done, 2 * i + (op.v0 + b + 3))
                            act.activation(blk(a_hi_t, 2 * i + b), blk(hidden, 2 * i + b), ACT.Copy).then_inc(a_hi_s, 1)
                        conv_at(1, nxt + 1, i, 2)
                elif op.kind == "upsq":
                    with act.Fori(0, 2) as i:
                        for s in range(2):
                            for b in range(2):
                                m = 2 * s + b
                                act.wait_ge(blk_mm, 4 * i + (2 * op.t0 + m + 1))
                                act.activation(blk(hidden, 4 * i + m), ps[m][:], ACT.Relu).then_inc(act1, 1)
                            conv_at(s, nxt + s, i, 2)
                            for b in range(2):
                                m = 2 * s + b
                                act.wait_ge(v_done, 4 * i + (op.v0 + m + 3))
                                act.activation(blk(a_hi_t, 4 * i + m), blk(hidden, 4 * i + m), ACT.Copy)\
                                   .then_inc(a_hi_s, 1)
                elif op.kind == "down":
                    for t in range(4):
                        if op.last:
                            for b in range(2):
                                square(op.n0, 2 * t + b, op.x0 + 2 * t + b + 1)
                        conv(t % 2, nxt + t)
                elif op.kind == "renorm":
                    root(op.n0)
                    for kb in range(DB):
                        square(op.n0 + 1, kb, op.x0 + kb + 1)
                elif op.kind == "final":
                    root(op.n0)
                elif op.kind == "attn":
                    natural_out(act, op, at_v, ACT.Copy, conv)
                    attn_act(act, op, conv)
                elif op.kind == "sgu":
                    act.wait_ge(h_lo_s, DB * op.h0)
                    act.dma_start(sg_wn, ins["sgu_w_s"][0].rearrange("g t s -> t g s")).then_inc(mix_d, 16)
                    act.dma_start(sg_mask, ins["consts"][:, C_CAUSAL * P:(C_CAUSAL + 1) * P]).then_inc(mix_d, 16)
                    for dst, name in ((sg_bs, "sgu_b_s"), (sg_g, "sgu_ln_g"), (sg_b, "sgu_ln_b")):
                        src = bass.AP(tensor=ins[name].tensor, offset=0, ap=[[0, P], [1, D]])
                        act.dma_start(dst, src).then_inc(mix_d, 16)
                    natural_out(act, op, sg_v, ACT.Gelu, conv)
                    for t in range(4, 8):
                        for b in range(2):
                            act.wait_ge(blk_mm, 2 * (op.t0 + t) + b + 1)
                            act.activation(blk(sg_u, 2 * (t - 4) + b), ps[2 * (t % 2) + b][:], ACT.Gelu)\
                               .then_inc(sg_ge, 1)
                        conv(t % 2, nxt + t)
                    for tb in range(TB):
                        act.wait_ge(sg_st, tb + 1)
                        act.activation(stat[:, 4 * tb + 2:4 * tb + 3], stat[:, 4 * tb + 1:4 * tb + 2], ACT.Sqrt,
                                       bias=eps).then_inc(sg_rt, 1)
                    for g in range(8):
                        act.wait_ge(sg_go, g + 1)
                        act.copy(blk(a_hi_t, g), sq[:, g % 2, :]).then_inc(a_hi_s, 1)
                elif op.kind == "hgrn":
                    hgrn_act(act, op, conv)

        def v_scratch(small_t):
            return small_t[:, 5:6]

        def attn_dve(dve, op, link):
            def combine(n):
                par, K = n % 2, (n % 4 + 1) * P
                st = stat[:, 8 * par:8 * par + 8]
                dve.wait_ge(exp_ok, 2 * n + 2)
                link(dve.reciprocal(st[:, 6:8], st[:, 4:6]))
                link(dve.tensor_tensor(st[:, 7:8], st[:, 7:8], neg_lam, ALU.mult))
                link(dve.tensor_scalar(at_s[:, par, 1, 0:K], at_s[:, par, 1, 0:K], st[:, 7:8], None, ALU.mult))
                dve.scalar_tensor_tensor(at_s[:, par, 0, 0:K], at_s[:, par, 0, 0:K], st[:, 6:7],
                                         at_s[:, par, 1, 0:K], ALU.mult, ALU.add).then_inc(at_ok, 1)

            def head_norm(hd):
                dve.wait_ge(o_root, hd + 1)
                link(dve.reciprocal(rstd[:], rstd[:]))
                dve.scalar_tensor_tensor(sq[:, 1, :], ps[6][:], sub_gain, rstd[:], ALU.mult, ALU.mult)\
                   .then_inc(o_ok, 1)
                dve.wait_ge(a_hi_s, op.a0 + hd + 1)
                dve.tensor_tensor(blk(a_lo_t, hd), sq[:, 1, :], blk(a_hi_t, hd).bitcast(F32), ALU.subtract)\
                   .then_inc(a_lo_s, 1)

            dve.wait_ge(bias_d, 16 * (1 + 2 * HEADS))
            for step in attn_sequence():
                if step[0] == "blk":
                    _, j, m = step
                    n = 4 * j + m
                    dve.wait_ge(qroot, n + 1)
                    link(dve.reciprocal(rstd[:], rstd[:]))
                    dve.scalar_tensor_tensor(at_qk[:, j % 2, m // 2, m % 2, :], ps[m][:], qk_gain[:, m // 2:m // 2 + 1],
                                             rstd[:], ALU.mult, ALU.mult).then_inc(qk_ok, 1)
                else:
                    n = step[1]
                    hd, i, par = n // 4, n % 4, n % 2
                    K = (i + 1) * P
                    st = stat[:, 8 * par:8 * par + 8]
                    dve.wait_ge(s_mm, n + 1)
                    if n >= 2:
                        dve.wait_ge(t_mm, n - 1)
                    for comp in range(2):
                        ins_ = dve.tensor_tensor_reduce(at_s[:, par, comp, 0:K], ps[4 + comp][:, 0:K],
                                                        at_bias[:, hd, S - K:S], 1.0, -3.0e38, ALU.add, ALU.max,
                                                        st[:, comp:comp + 1])
                        ins_.then_inc(s_rd, 1)
                    dve.wait_ge(s_rd, 2 * n + 2)
                    dve.tensor_scalar(st[:, 2:4], st[:, 0:2], -1.0, None, ALU.mult).then_inc(mx_ok, 1)
                    if n >= 1:
                        combine(n - 1)
                    if n >= 4 and n % 4 == 0:
                        head_norm(n // 4 - 1)
            combine(31)
            head_norm(7)
            link(dve.memset(ssq[:], 0.0))

        def hgrn_dve(dve, op, link):
            lbv = vec[:, V_LB:V_LB + 8]
            link(dve.tensor_tensor(lb, lbv, lbv, ALU.subtract))
            link(dve.tensor_scalar(one_lb, lb, 1.0, None, ALU.add))
            link(dve.reciprocal(lb, one_lb))
            link(dve.tensor_tensor(lb, one_lb, lb, ALU.mult))
            link(dve.tensor_tensor(lb, lb, lb, ALU.subtract))
            link(dve.tensor_scalar(one_lb, lb, -1.0, 1.0, ALU.mult, ALU.add))
            link(dve.memset(hidden[:, 2048:4096], 0.0))
            dve.wait_ge(mix_d, 16 * 6)
            for step in hgrn_sequence():
                if step[0] == "unit":
                    _, j, u = step
                    kind, b = HG_UNITS[u]
                    par, hd = j % 2, 2 * j + b
                    if kind == "q":
                        dve.wait_ge(hg_ev, 8 * j + u + 1)
                        link(dve.tensor_scalar(hg_f[:, par, b, :], hg_f[:, par, b, :], one_lb[:, hd:hd + 1],
                                               lb[:, hd:hd + 1], ALU.mult, ALU.add))
                        link(dve.tensor_scalar(hg_k[:, par, b, :], hg_k[:, par, b, :], one_lb[:, hd:hd + 1], None,
                                               ALU.mult))
                        link(dve.tensor_scalar(hg_q[:, par, b, :], hg_q[:, par, b, :], H_SCALE, None, ALU.mult))
                    continue
                _, hd, s = step
                par, b = (hd // 2) % 2, hd % 2
                n = hd * (LEVELS + 3) + s
                F, K, Q = hg_f[:, par, b, :], hg_k[:, par, b, :], hg_q[:, par, b, :]
                if s == 0:
                    link(dve.memset(hg_l, 1.0))
                    if n >= 2:
                        dve.wait_ge(hg_mm, n - 1)
                    link(dve.tensor_copy(hg_qe[:, n % 2, :], Q))
                    dve.tensor_copy(hg_ke[:, n % 2, :], K).then_inc(hg_qk, 1)
                elif s <= LEVELS + 2:
                    h = 1 << (s - 1)

                    def lower(ap):
                        return ap.rearrange("p (n c h) -> p n c h", c=2, h=h)[:, :, 0, :]

                    def upper(ap):
                        return ap.rearrange("p (n c h) -> p n c h", c=2, h=h)[:, :, 1, :]

                    nb = S // (2 * h)
                    low_end = bcast(F[:, h - 1:h], [[2 * h, nb], [0, h]])
                    up_end = bcast(F[:, 2 * h - 1:2 * h], [[2 * h, nb], [0, h]])
                    if n >= 2:
                        dve.wait_ge(hg_mm, n - 1)
                    dve.tensor_tensor(upper(hg_qe[:, n % 2, :]), upper(Q), upper(F), ALU.mult)
                    dve.tensor_tensor(lower(hg_ke[:, n % 2, :]), lower(K), lower(hg_l), ALU.mult).then_inc(hg_qk, 1)
                    dve.wait_ge(hg_qk, n + 1)
                    if s < LEVELS + 2:
                        link(dve.tensor_tensor(lower(hg_l), lower(hg_l), up_end, ALU.mult))
                        link(dve.tensor_tensor(upper(F), upper(F), low_end, ALU.mult))
                if 1 <= s <= LEVELS + 1:
                    m = s - 1
                    dve.wait_ge(hg_mm, n)
                    src = ps[4 + m % 2][:].rearrange("p (a t) -> p a t", t=P)
                    dst = bcast(hg_p[:, 0:P], [[S + P, TB], [1, P]])
                    if m == 0:
                        if hd:
                            dve.wait_ge(o_mm, 8 + hd)
                        ins_ = dve.tensor_tensor(dst, src, bcast(ident[:], [[0, TB], [1, P]]), ALU.mult)
                    else:
                        ins_ = dve.copy_predicated(dst, bcast(hg_mask[:, m - 1, :], [[0, TB], [1, P]]).bitcast(I32), src)
                    ins_.then_inc(hg_pc, 1)
                    dve.wait_ge(hg_pc, hd * (LEVELS + 1) + s)
                if s == LEVELS + 3:
                    if hd:
                        dve.wait_ge(a_lo_s, op.a0 + hd)
                    dve.wait_ge(o_root, 8 + hd + 1)
                    link(dve.reciprocal(rstd[:], rstd[:]))
                    link(dve.scalar_tensor_tensor(sq[:, 0, :], ps[6][:], vec[:, V_ON + hd:V_ON + hd + 1], rstd[:],
                                                  ALU.mult, ALU.mult))
                    dve.tensor_tensor(sq[:, 1, :], sq[:, 0, :], hg_g[:, par, b, :], ALU.mult).then_inc(o_ok, 1)
                    dve.wait_ge(a_hi_s, op.a0 + hd + 1)
                    dve.tensor_tensor(blk(a_lo_t, hd), sq[:, 1, :], blk(a_hi_t, hd).bitcast(F32), ALU.subtract)\
                       .then_inc(a_lo_s, 1)

            link(dve.memset(ssq[:], 0.0))

        @block.vector
        def _(dve):
            links = [0]

            def link(ins_):
                links[0] += 1
                ins_.then_inc(chain, 1)
                dve.wait_ge(chain, links[0])

            def ssq_add(n, kb):
                dve.wait_ge(sq_done, 8 * n + kb + 1)
                if 8 * n + kb:
                    dve.wait_ge(ssq_done, 8 * n + kb)
                dve.tensor_tensor(ssq[:], ssq[:], sq[:, kb % 2, :], ALU.add).then_inc(ssq_done, 1)

            def rstd_make(n, clear=True):
                dve.wait_ge(root_ok, n + 1)
                link(dve.reciprocal(rstd[:], rstd[:]))
                if clear:
                    link(dve.memset(ssq[:], 0.0))

            def ada_chunk(slot, c, acc):
                dst = ada_acc[:, acc]
                for kb in range(KB):
                    if kb == 0:
                        dve.wait_ge(ada_in[slot], 16 * (c // 2) + 16 if isinstance(c, int) else c)
                    else:
                        dve.wait_ge(ada_ch, 8 * c + kb)
                    if kb == 0:
                        dve.tensor_scalar(dst, ada_raw[:, slot, kb, :], cact[:, kb:kb + 1], None, ALU.mult)\
                           .then_inc(ada_ch, 1)
                    else:
                        dve.scalar_tensor_tensor(dst, ada_raw[:, slot, kb, :], cact[:, kb:kb + 1], dst,
                                                 ALU.mult, ALU.add).then_inc(ada_ch, 1)

            def ada_loop_chunk(slot, c0, i, step, acc0):
                dst = ada_acc[:, bass.ds(i * (step * TW) + acc0 * TW, TW)]
                for kb in range(KB):
                    if kb == 0:
                        dve.wait_ge(ada_in[slot], 8 * step * i + 16 * (c0 // 2 + 1))
                        dve.tensor_scalar(dst, ada_raw[:, slot, kb, :], cact[:, kb:kb + 1], None, ALU.mult)\
                           .then_inc(ada_ch, 1)
                    else:
                        dve.wait_ge(ada_ch, 8 * step * i + (8 * c0 + kb))
                        dve.scalar_tensor_tensor(dst, ada_raw[:, slot, kb, :], cact[:, kb:kb + 1], dst,
                                                 ALU.mult, ALU.add).then_inc(ada_ch, 1)

            def derive_gain(layer, i, ln):
                m = (3 * i + 1) * DB
                dve.scalar_tensor_tensor(gain[:, layer, i, :], mod[:, layer, m:m + DB], 1.0,
                                         vec[:, V_LN + 16 * i + 8 * layer:V_LN + 16 * i + 8 * layer + DB],
                                         ALU.add, ALU.mult)

            def derive_half(layer, i):
                m = (3 * i + 2) * DB
                dve.tensor_scalar(half[:, layer, i // 2, :], mod[:, layer, m:m + DB], 0.5, None, ALU.mult)

            def ada_fin(layer, m0, m1, count, derive):
                dve.wait_ge(ada_mm, count)
                link(dve.tensor_tensor(mod[:, layer, m0:m1], ps[7][:, m0:m1],
                                       vec[:, V_ADA[layer] + m0:V_ADA[layer] + m1], ALU.add))
                for kind, i in derive:
                    derive_gain(layer, i, None) if kind == "g" else derive_half(layer, i)
                dve.memset(small[:, 5:6], 0.0).then_inc(mod_ok, 1)
                dve.wait_ge(mod_ok, count)

            dve.memset(eps, EPS)
            dve.memset(ssq[:], 0.0)
            dve.memset(hidden[BUCKETS:BUCKETS + 1, 768:776], NEG)
            dve.memset(ones[:], 1.0).then_inc(init_d, 1)
            dve.wait_ge(init_p, 1)
            dve.tensor_copy(vec[:, 0:80], ps[0][:, 0:80])
            dve.tensor_copy(vec[:, 128:200], ps[0][:, 128:200])
            dve.tensor_copy(vec[:, V_LN:V_COLS], ps[0][:, V_LN:V_COLS]).then_inc(init_d, 1)
            dve.wait_ge(init_d, 2)
            dve.memset(small[:, 5:6], 0.0).then_inc(init_d, 1)
            dve.wait_ge(xin, 16 * 11)
            for i in range(2):
                link(dve.tensor_tensor(hidden[:, 3072 + 64 * i:3136 + 64 * i], hidden[:, 512 + 128 * i:576 + 128 * i],
                                       hidden[:, 576 + 128 * i:640 + 128 * i], ALU.mult))
            link(dve.tensor_reduce(small[:, 6:8], hidden[:, 3072:3200].rearrange("p (a b) -> p a b", b=64),
                                   mybir.AxisListType.X, ALU.add))
            dve.memset(v_scratch(small), 0.0).then_inc(init_d, 1)
            dve.tensor_scalar(sub_gain, vec[:, V_SUB:V_SUB + 1], 1.0 - LAMBDA_INIT, None, ALU.mult)
            dve.tensor_scalar(qk_gain[:, 0:1], qk_gain[:, 0:1], Q_SCALE, None, ALU.mult)
            dve.wait_ge(bias_sb, 1)
            dve.tensor_copy(hidden[0:HEADS, 2048:2560], ps[1][0:HEADS, :])
            dve.tensor_copy(hidden[0:HEADS, 2560:2048 + STRIP], ps[2][0:HEADS, 0:P]).then_inc(bias_sb, 1)
            for kb in range(DB):
                dve.wait_ge(init_p, 2 + kb)
                dve.tensor_copy(blk(x, kb), ps[kb][:]).then_inc(x_upd, 1)
                if kb >= 1:
                    ssq_add(0, kb - 1)
            ssq_add(0, 7)
            dve.wait_ge(init_a, 2)
            link(dve.tensor_tensor(neg_lam, small[:, 7:8], small[:, 6:7], ALU.subtract))
            link(dve.tensor_scalar(neg_lam, neg_lam, -LAMBDA_INIT, None, ALU.add))
            dve.memset(small[:, 5:6], 0.0).then_inc(v_done, 2)
            for c in range(8):
                ada_chunk(c % 2, c, slice(c * TW, (c + 1) * TW))
            ada_fin(0, 0, 16, 1, [("g", 0)])

            for op in ops:
                if op.kind == "norm":
                    rstd_make(op.n0)

                    def h_low(kb):
                        dve.wait_ge(h_hi_s, DB * op.h0 + kb + 1)
                        u = hidden[:, S * (kb % 2):S * (kb % 2) + S] if op.shift else sq[:, kb % 2, :]
                        dve.tensor_tensor(blk(h_lo, kb), u, blk(h_hi, kb).bitcast(F32), ALU.subtract)\
                           .then_inc(h_lo_s, 1)

                    for kb in range(DB):
                        t = sq[:, kb % 2, :]
                        if op.shift:
                            dve.tensor_tensor(t, blk(x, kb), rstd[:], ALU.mult).then_inc(h_t, 1)
                            dve.wait_ge(h_t, DB * op.h0 + kb + 1)
                            link(dve.tensor_scalar(hidden[:, S * (kb % 2):S * (kb % 2) + S], t, gain_col(op, kb),
                                                   shift_col(op, kb), ALU.mult, ALU.add))
                        else:
                            if kb >= 2:
                                dve.wait_ge(h_lo_s, DB * op.h0 + kb - 1)
                            dve.scalar_tensor_tensor(t, blk(x, kb), gain_col(op, kb), rstd[:], ALU.mult,
                                                     ALU.mult).then_inc(h_t, 1)
                            dve.wait_ge(h_t, DB * op.h0 + kb + 1)
                        if kb:
                            h_low(kb - 1)
                    h_low(DB - 1)
                elif op.kind in ("renorm", "final"):
                    rstd_make(op.n0)
                    for kb in range(DB):
                        ins_ = dve.scalar_tensor_tensor(blk(x, kb), blk(x, kb), gain_col(op, kb), rstd[:],
                                                        ALU.mult, ALU.mult)
                        ins_.then_inc(x_upd, 1)
                        if op.kind == "renorm" and kb:
                            ssq_add(op.n0 + 1, kb - 1)
                    if op.kind == "renorm":
                        ssq_add(op.n0 + 1, 7)
                    else:
                        for tb in range(TB):
                            for hf in range(2):
                                n = 2 * tb + hf
                                dve.wait_ge(fin_t, n + 1)
                                dve.tensor_copy(at_v[:, tb, hf * S:(hf + 1) * S], ps[n % 4][:]).then_inc(fin_c, 1)
                elif op.kind == "ada4":
                    for c in range(8, 12):
                        ada_chunk(c % 2, c, slice((c - 8) * TW, (c - 7) * TW))
                elif op.kind == "adafin":
                    if not op.skip:
                        if op.fin == 2:
                            derive = [("h", 0)]
                        elif op.fin == 4:
                            derive = [("g", 1), ("g", 2), ("h", 2)]
                        elif op.fin == 7:
                            derive = [("g", 0), ("h", 0), ("g", 1), ("g", 2), ("h", 2)]
                        else:
                            derive = []
                        ada_fin(op.layer, op.m0, op.m1, op.fin, derive)
                elif op.kind == "up":
                    with dve.Fori(0, op.nb // 2) as i:
                        for m in range(op.ada):
                            ada_loop_chunk(m % 2, op.c0 + m, i, op.ada, m)
                        for b in range(2):
                            dve.wait_ge(act1, 2 * i + (op.v0 + b + 1))
                            dve.tensor_tensor(blk(hidden, 2 * i + b), blk(hidden, 2 * i + b), ps[2 + b][:],
                                              ALU.mult).then_inc(v_done, 1)
                        for b in range(2):
                            dve.wait_ge(a_hi_s, 2 * i + (op.a0 + b + 1))
                            dve.tensor_tensor(blk(a_lo_t, 2 * i + b), blk(hidden, 2 * i + b),
                                              blk(a_hi_t, 2 * i + b).bitcast(F32), ALU.subtract).then_inc(a_lo_s, 1)
                elif op.kind == "upsq":
                    with dve.Fori(0, 2) as i:
                        for s in range(2):
                            for m in (2 * s, 2 * s + 1):
                                dve.wait_ge(act1, 4 * i + (op.v0 + m + 1))
                                dve.tensor_tensor(blk(hidden, 4 * i + m), blk(hidden, 4 * i + m),
                                                  blk(hidden, 4 * i + m), ALU.mult).then_inc(v_done, 1)
                            for m in (2 * s, 2 * s + 1):
                                dve.wait_ge(a_hi_s, 4 * i + (op.a0 + m + 1))
                                dve.tensor_tensor(blk(a_lo_t, 4 * i + m), blk(hidden, 4 * i + m),
                                                  blk(a_hi_t, 4 * i + m).bitcast(F32), ALU.subtract)\
                                   .then_inc(a_lo_s, 1)
                elif op.kind == "down":
                    for nb in range(DB):
                        dve.wait_ge(blk_mm, 2 * op.t0 + nb + 1)
                        xb = blk(x, nb)
                        if op.gate:
                            ins_ = dve.scalar_tensor_tensor(xb, ps[4 + nb % 2][:], gate_col(op, nb), xb,
                                                            ALU.mult, ALU.add)
                        else:
                            ins_ = dve.tensor_tensor(xb, ps[4 + nb % 2][:], xb, ALU.add)
                        ins_.then_inc(x_upd, 1)
                        if op.last and nb:
                            ssq_add(op.n0, nb - 1)
                    if op.last:
                        ssq_add(op.n0, 7)
                elif op.kind == "attn":
                    attn_dve(dve, op, link)
                elif op.kind == "sgu":
                    dve.wait_ge(mix_d, 16 * 5)
                    for hf in range(2):
                        dve.wait_ge(sg_tr, hf + 1)
                        src = ps[4 + hf][:].rearrange("p (g t) -> p g t", t=P)
                        dve.tensor_tensor(sg_ws[:, 4 * hf:4 * hf + 4, :], src, bcast(sg_mask, [[0, 4], [1, P]]),
                                          ALU.mult).then_inc(sg_wm, 1)
                    for tb in range(TB):
                        v = sg_v[:, tb, :]
                        st = stat[:, 16:28]
                        dve.wait_ge(nat_ev, 16 + 12 + tb + 1)
                        for hf in range(2):
                            ins_ = dve.bn_stats(st[:, 6 * hf:6 * hf + 6], v[:, hf * S:(hf + 1) * S])
                        link(ins_)
                        dve.bn_aggr(stat[:, 4 * tb:4 * tb + 2], st).then_inc(sg_st, 1)
                        dve.wait_ge(sg_rt, tb + 1)
                        link(dve.reciprocal(stat[:, 4 * tb + 3:4 * tb + 4], stat[:, 4 * tb + 2:4 * tb + 3]))
                        link(dve.tensor_scalar(v, v, stat[:, 4 * tb:4 * tb + 1], stat[:, 4 * tb + 3:4 * tb + 4],
                                               ALU.subtract, ALU.mult))
                        link(dve.tensor_tensor(v, v, sg_g, ALU.mult))
                        dve.tensor_tensor(v, v, sg_b, ALU.add).then_inc(sg_vn, 1)
                    def low(g):
                        dve.wait_ge(a_hi_s, op.a0 + g + 1)
                        dve.tensor_tensor(blk(a_lo_t, g), sq[:, g % 2, :], blk(a_hi_t, g).bitcast(F32),
                                          ALU.subtract).then_inc(a_lo_s, 1)

                    for g in range(8):
                        if g >= 2:
                            dve.wait_ge(a_lo_s, op.a0 + g - 1)
                        dve.wait_ge(sg_mm, g + 1)
                        mixed = ps[6 + g % 2][:].rearrange("p (n t) -> p n t", t=P)
                        tmp = sq[:, g % 2, :]
                        dve.tensor_tensor(tmp.rearrange("p (n t) -> p n t", t=P), mixed,
                                          bcast(sg_bs[:, g * P:(g + 1) * P], [[0, TB], [1, P]]), ALU.add)\
                           .then_inc(sg_ev, 1)
                        dve.wait_ge(sg_ev, g + 1)
                        dve.wait_ge(sg_ge, g + 1)
                        dve.tensor_tensor(tmp, tmp, blk(sg_u, g), ALU.mult).then_inc(sg_go, 1)
                        if g:
                            low(g - 1)
                    low(7)
                elif op.kind == "hgrn":
                    hgrn_dve(dve, op, link)

        def op_norm(op):
            return op

        def op_operand(op):
            return op.a0 - op.kb

        def attn_pe(pe, op, unit):
            def turn(n):
                par, i = n % 2, n % 4
                pe.wait_ge(at_ok, n + 1)
                if n:
                    pe.wait_ge(t_ev, n)
                if n and i == 0:
                    pe.wait_ge(o_root, n // 4)
                for kb in range(i + 1):
                    mm = pe.transpose(ps[7][:, kb * P:(kb + 1) * P], at_s[:, par, 0, kb * P:(kb + 1) * P], ident[:])
                mm.then_inc(t_mm, 1)
                if i == 3:
                    output(n // 4)

            def output(hd):
                pe.wait_ge(t_ev, 4 * hd + 4)
                for kb in range(TB):
                    mm = pe.matmul(ps[6][:, kb * P:S], at_v[:, kb, hd * P:(hd + 1) * P], at_tr[:, kb, kb * P:S],
                                   start=kb == 0, stop=kb == TB - 1)
                mm.then_inc(o_mm, 1)
                pe.wait_ge(o_sq, hd + 1)
                pe.matmul(ps[7][:], ones[:], ssq[:], start=True, stop=True).then_inc(o_ss, 1)

            for step in attn_sequence():
                if step[0] == "blk":
                    _, j, m = step
                    n = 4 * j + m
                    if m % 2 == 0:
                        pe.wait_ge(w_lo, op.t0 + 4 + 2 * j + m // 2 + 1)
                    if n >= 4:
                        pe.wait_ge(qk_ok, n - 3)
                    else:
                        pe.wait_ge(nat_ev, 16)
                    unit(ps[m][:], m // 2, m % 2, h_hi, h_lo)
                    pe.wait_ge(qsq, n + 1)
                    outputs = (8 * (j - 1) + 2 * m - 1) // 4
                    if outputs > 0:
                        pe.wait_ge(o_ok, outputs)
                    pe.matmul(ps[6][:], blk64[:], sq[:, 0, :], start=True, stop=True).then_inc(qss, 1)
                else:
                    n = step[1]
                    hd, i = n // 4, n % 4
                    j, K = hd // 2, (i + 1) * P
                    pe.wait_ge(qk_ok, 4 * j + 4)
                    if n:
                        pe.wait_ge(s_rd, 2 * n)
                    for comp in range(2):
                        rows = slice(64 * comp, 64 * comp + 64)
                        mm = pe.matmul(ps[4 + comp][:, 0:K], at_qk[rows, j % 2, 0, hd % 2, i * P:(i + 1) * P],
                                       at_qk[rows, j % 2, 1, hd % 2, 0:K], start=True, stop=True)
                    mm.then_inc(s_mm, 1)
                    if n >= 1:
                        turn(n - 1)
            turn(31)

        def hgrn_pe(pe, op, unit, nat_unit):
            for step in hgrn_sequence():
                if step[0] == "unit":
                    _, j, u = step
                    kind, b = HG_UNITS[u]
                    if j == 0 and u == 0:
                        pe.wait_ge(h_lo_s, DB * op.h0)
                    if u % 2 == 0:
                        pe.wait_ge(w_lo, op.t0 + 4 * j + u // 2 + 1)
                    if 8 * j + u:
                        last_use = {0: 8 * j, 1: 8 * j, 2: 8 * j + 2, 3: 8 * j + 2, 4: 8 * j + 4, 5: 8 * j + 4,
                                    6: 8 * j + 4, 7: 8 * j + 4}[u]
                        if last_use:
                            pe.wait_ge(hg_ev, last_use)
                    slot = (u // 2) % 2
                    if kind == "i":
                        nat_unit(slot, b, 0)
                    else:
                        unit(ps[b + (2 if kind == "q" else 0)][:], slot, b, h_hi, h_lo)
                    continue
                _, hd, s = step
                par, b = (hd // 2) % 2, hd % 2
                n = hd * (LEVELS + 3) + s
                if s <= LEVELS + 2:
                    pe.wait_ge(hg_qk, n + 1)
                    ke, qe = hg_ke[:, n % 2, :], hg_qe[:, n % 2, :]
                    if s <= LEVELS:
                        if s >= 2:
                            pe.wait_ge(hg_pc, hd * (LEVELS + 1) + s - 1)
                        elif hd:
                            pe.wait_ge(hg_pc, hd * (LEVELS + 1))
                        for c in range(TB):
                            tok = slice(c * P, (c + 1) * P)
                            mm = pe.matmul(ps[4 + s % 2][:, tok], ke[:, tok], qe[:, tok], start=True, stop=True)
                    elif s == LEVELS + 1:
                        if hd:
                            pe.wait_ge(o_ok, 8 + hd)
                        for c in range(2):
                            mm = pe.matmul(ps[6][:, c * P:(c + 1) * P], ke[:, 2 * c * P:(2 * c + 1) * P],
                                           qe[:, (2 * c + 1) * P:(2 * c + 2) * P], start=True, stop=True)
                    else:
                        if hd:
                            pe.wait_ge(o_root, 8 + hd)
                        for c in range(2):
                            mm = pe.matmul(ps[7][:, c * 2 * P:(c + 1) * 2 * P], ke[:, c * P:(c + 1) * P],
                                           qe[:, 2 * P:4 * P], start=True, stop=True)
                    mm.then_inc(hg_mm, 1)
                else:
                    pe.wait_ge(hg_pc, (hd + 1) * (LEVELS + 1))
                    pe.wait_ge(hg_far, 2 * hd + 2)
                    for c in range(TB):
                        mm = pe.matmul(ps[6][:, c * P:S], hg_v[:, par, c, b * P:(b + 1) * P],
                                       hg_p[:, c * S + c * P:(c + 1) * S], start=c == 0, stop=c == TB - 1)
                    mm.then_inc(o_mm, 1)
                    pe.wait_ge(o_sq, 8 + hd + 1)
                    pe.matmul(ps[7][:], ones[:], ssq[:], start=True, stop=True).then_inc(o_ss, 1)

        @block.tensor
        def _(pe):
            def product(dst, w_h, w_l, m_h, m_l, first, last):
                pe.matmul(dst, w_h, m_h, start=first, stop=False)
                pe.matmul(dst, w_h, m_l, start=False, stop=False)
                return pe.matmul(dst, w_l, m_h, start=False, stop=last)

            def unit(dst, slot, b, m_hi, m_lo, kbs=KB, wait_k=None):
                for kb in range(kbs):
                    if wait_k:
                        wait_k(kb)
                    w = (w_hi_t[:, slot, kb, b * P:(b + 1) * P], w_lo_t[:, slot, kb, b * P:(b + 1) * P])
                    last = product(dst, w[0], w[1], blk(m_hi, kb), blk(m_lo, kb), kb == 0, kb == kbs - 1)
                last.then_inc(blk_mm, 1)

            def nat_unit(slot, half_, banks):
                for tb in (2 * half_, 2 * half_ + 1):
                    for kb in range(KB):
                        tok = slice(kb * S + tb * P, kb * S + (tb + 1) * P)
                        dst = ps[banks + tb][:, 0:TW]
                        pe.matmul(dst, h_hi[:, tok], w_hi_t[:, slot, kb, :], start=kb == 0, stop=False)
                        pe.matmul(dst, h_hi[:, tok], w_lo_t[:, slot, kb, :], start=False, stop=False)
                        last = pe.matmul(dst, h_lo[:, tok], w_hi_t[:, slot, kb, :], start=False, stop=kb == KB - 1)
                last.then_inc(blk_mm, 1)

            def h_ready(op):
                return lambda kb: pe.wait_ge(h_lo_s, DB * (op.h0 - 1) + kb + 1)

            def sum_squares(n):
                pe.wait_ge(ssq_done, 8 * (n + 1))
                pe.matmul(ps[6][:], ones[:], ssq[:], start=True, stop=True).then_inc(ssum_mm, 1)

            def ada_sum(m0, m1, chunks, fin):
                if fin > 1:
                    pe.wait_ge(mod_ok, fin - 1)
                pe.wait_ge(ada_ch, 8 * chunks)
                for m in range(m0, m1):
                    a = (m - m0) * P
                    mm = pe.matmul(ps[7][:, m:m + 1], ada_acc[:, a:a + P], ones[:, 0:1], start=True, stop=True)
                mm.then_inc(ada_mm, 1)

            pe.wait_ge(init_d, 1)
            pe.wait_ge(cst_in, 16 * 19)
            for grp, (c0, n) in enumerate(((0, 80), (128, 72), (V_LN, V_COLS - V_LN))):
                mm = pe.transpose(ps[0][:, c0:c0 + n], vrow[0:n, grp, :], ident[0:n, 0:n])
            mm.then_inc(init_p, 1)
            pe.wait_ge(xin, 16 * 11)
            table, onehot = hidden[0:BUCKETS + 1, 768:776], hidden[0:BUCKETS + 1, 1024:1024 + STRIP]
            pe.matmul(ps[1][0:HEADS, :], table, onehot[:, 0:S], start=True, stop=True)
            pe.matmul(ps[2][0:HEADS, 0:P], table, onehot[:, S:STRIP], start=True, stop=True).then_inc(bias_sb, 1)
            pe.wait_ge(init_d, 2)
            for db in range(DB):
                if db == 1:
                    pe.wait_ge(bias_sb, 2)
                for tb in range(TB):
                    mm = pe.transpose(ps[db][:, tb * P:(tb + 1) * P], x_nat[:, tb, db * P:(db + 1) * P], ident[:])
                mm.then_inc(init_p, 1)
            pe.wait_ge(x_upd, 8)
            sum_squares(0)
            ada_sum(0, 16, 8, 1)

            for op in ops:
                if op.kind == "adafin":
                    if not op.skip:
                        ada_sum(op.m0, op.m1, op.ce, op.fin)
                elif op.kind == "up":
                    with pe.Fori(0, op.nb // 2) as i:
                        for s in range(2):
                            pe.wait_ge(w_lo, 2 * i + (op.t0 + s + 1))
                            for b in range(2):
                                if s == 0:
                                    pe.wait_ge(v_done, 2 * i + (op.v0 + b + 1))
                                unit(ps[2 * s + b][:], s, b, h_hi, h_lo,
                                     wait_k=h_ready(op_norm(op)) if s == 0 and b == 0 else None)
                elif op.kind == "upsq":
                    with pe.Fori(0, 2) as i:
                        for s in range(2):
                            pe.wait_ge(w_lo, 2 * i + (op.t0 + s + 1))
                            for b in range(2):
                                pe.wait_ge(v_done, 4 * i + (op.v0 + 2 * s + b - 1))
                                unit(ps[2 * s + b][:], s, b, h_hi, h_lo,
                                     wait_k=h_ready(op_norm(op)) if s == 0 and b == 0 else None)
                elif op.kind == "down":
                    a0 = op_operand(op)
                    with pe.Fori(0, 2) as i:
                        for s in range(2):
                            pe.wait_ge(w_lo, 2 * i + (op.t0 + s + 1))
                            for b in range(2):
                                pe.wait_ge(x_upd, 4 * i + (op.x0 + 2 * s + b - 1))
                                unit(ps[4 + b][:], s, b, a_hi_t, a_lo_t, kbs=op.kb,
                                     wait_k=(lambda kb: pe.wait_ge(a_lo_s, a0 + kb + 1)) if s == b == 0 else None)
                    if op.last:
                        sum_squares(op.n0)
                elif op.kind == "renorm":
                    sum_squares(op.n0 + 1)
                elif op.kind == "final":
                    for tb in range(TB):
                        for hf in range(2):
                            n = 2 * tb + hf
                            pe.wait_ge(x_upd, op.x0 + 4 * hf + 4)
                            if n >= 4:
                                pe.wait_ge(fin_c, n - 3)
                            for d in range(4):
                                db = 4 * hf + d
                                mm = pe.transpose(ps[n % 4][:, d * P:(d + 1) * P],
                                                  x[:, db * S + tb * P:db * S + (tb + 1) * P], ident[:])
                            mm.then_inc(fin_t, 1)
                elif op.kind in ("attn", "sgu"):
                    pe.wait_ge(h_lo_s, DB * op.h0)
                    nat0 = 0 if op.kind == "attn" else 16
                    for t in range(4):
                        pe.wait_ge(w_lo, op.t0 + t + 1)
                        if t >= 2:
                            pe.wait_ge(nat_ev, nat0 + 4 * (t - 1))
                        for hf in range(2):
                            nat_unit(t % 2, hf, 4 * (t % 2))
                    if op.kind == "attn":
                        attn_pe(pe, op, unit)
                    else:
                        pe.wait_ge(mix_d, 16 * 5)
                        pe.wait_ge(nat_ev, nat0 + 16)
                        for hf in range(2):
                            for g in range(4):
                                mm = pe.transpose(ps[4 + hf][:, g * P:(g + 1) * P], sg_wn[:, 4 * hf + g, :], ident[:])
                            mm.then_inc(sg_tr, 1)
                        for t in range(4):
                            pe.wait_ge(w_lo, op.t0 + 4 + t + 1)
                            for b in range(2):
                                n = 2 * t + b
                                if n >= 4:
                                    pe.wait_ge(sg_ge, n - 3)
                                unit(ps[n % 4][:], t % 2, b, h_hi, h_lo)
                        pe.wait_ge(sg_wm, 2)
                        pe.wait_ge(sg_vn, TB)
                        for g in range(8):
                            if g >= 2:
                                pe.wait_ge(sg_ev, g - 1)
                            for n in range(TB):
                                mm = pe.matmul(ps[6 + g % 2][:, n * P:(n + 1) * P], sg_v[:, n, g * P:(g + 1) * P],
                                               sg_ws[:, g, :], start=True, stop=True)
                            mm.then_inc(sg_mm, 1)
                elif op.kind == "hgrn":
                    hgrn_pe(pe, op, unit, nat_unit)

INPUTS = [
    "x", "c", "rel_bias", "ada_w", "ada_b", "ln_ffn1", "ffn1_wg", "ffn1_wu", "ffn1_wd", "ln_mix", "ln_ffn2",
    "ffn2_wg", "ffn2_wu", "ffn2_wd", "ln_out", "attn_w_qkv", "attn_q_norm", "attn_k_norm", "attn_lq1", "attn_lk1",
    "attn_lq2", "attn_lk2", "attn_subln", "attn_w_o", "sgu_w_in", "sgu_ln_g", "sgu_ln_b", "sgu_w_s", "sgu_b_s",
    "sgu_w_out", "norm_mix_2", "norm_mlp_2", "norm_final_2", "hgrn_w_in_2", "hgrn_lower_bound_2",
    "hgrn_out_norm_2", "hgrn_w_out_2", "mlp_w1_2", "mlp_w2_2",
]


def kernel(**inputs):
    import concourse.bacc as bacc
    from concourse.bass_utils import run_bass_kernel_spmd as run

    nc = bacc.Bacc("TRN2", target_bir_lowering=False, num_devices=1)
    consts, onehot = shape_constants()
    host = {name: np.ascontiguousarray(inputs[name]) for name in INPUTS}
    host["consts"], host["onehot"] = consts, onehot
    arrays, aps = {}, {}
    for name, a in host.items():
        arrays[f"in_{name}"] = a
        aps[name] = nc.dram_tensor(f"in_{name}", a.shape, mybir.dt.from_np(a.dtype), kind="ExternalInput").ap()
    out = nc.dram_tensor("out", (1, S, D), F32, kind="ExternalOutput").ap()
    build_program(nc, aps, out)
    r = run(nc, [arrays], core_ids=[0])
    return r.results[0]["out"]
```
